# Optimizing a Trainium2 kernel written in Bass

```python
import math
import jax, jax.numpy as jnp
from jax import lax
import numpy as np

D_MODEL = 1024
BATCH = 1
SEQ = 256
DEPTH = 2

D_FF = 2816
HEAD_DIM_A = 64
N_HEADS_A = 8
N_KV_HEADS_A = 2
GROUP_A = N_HEADS_A // N_KV_HEADS_A
WINDOW = 128
BLOCK = 128
N_HEADS_B = 8
Q_LORA_RANK = 256
KV_LORA_RANK = 128
QK_NOPE_DIM = 64
QK_ROPE_DIM = 32
QK_DIM_B = QK_NOPE_DIM + QK_ROPE_DIM
V_DIM_B = 64
ROPE_BASE = 10000.0
WIDTH_A = N_HEADS_A * HEAD_DIM_A
WIDTH_B = N_HEADS_B * V_DIM_B
IN_SPLITS = (WIDTH_A, N_KV_HEADS_A * HEAD_DIM_A, N_KV_HEADS_A * HEAD_DIM_A,
             Q_LORA_RANK, KV_LORA_RANK, QK_ROPE_DIM, D_MODEL, D_MODEL)
IN_WIDTH = sum(IN_SPLITS)
IN_OFFSETS = tuple(int(o) for o in np.cumsum(IN_SPLITS)[:-1])
EPS = 1e-6
NEG = -1e30

kernel_name = "hybrid_swa_sink_mla_gated_macaron"

def rms_norm(x, g):
    xf = x.astype(jnp.float32)
    y = xf * lax.rsqrt(jnp.mean(xf * xf, axis=-1, keepdims=True) + EPS)
    return (y * g.astype(jnp.float32)).astype(x.dtype)

def swiglu(x, w_gate, w_up, w_down):
    return (jax.nn.silu(x @ w_gate) * (x @ w_up)) @ w_down

def apply_rope(x, cos, sin):
    half = x.shape[-1] // 2
    x1, x2 = x[..., :half], x[..., half:]
    return jnp.concatenate([x1 * cos - x2 * sin, x2 * cos + x1 * sin], axis=-1)

def alibi_slopes(n_heads):
    return jnp.exp2(-8.0 * (jnp.arange(n_heads, dtype=jnp.float32) + 1.0) / n_heads)

def swa_attention(q, k, v, positions, q_gain, k_gain, sinks):
    B, S = q.shape[0], q.shape[1]
    nb = S // BLOCK
    q = rms_norm(q, q_gain)
    k = rms_norm(k, k_gain)
    qb = q.reshape(B, nb, BLOCK, N_KV_HEADS_A, GROUP_A, HEAD_DIM_A)
    kb = k.reshape(B, nb, BLOCK, N_KV_HEADS_A, HEAD_DIM_A)
    vb = v.reshape(B, nb, BLOCK, N_KV_HEADS_A, HEAD_DIM_A)
    pad5 = ((0, 0), (1, 0), (0, 0), (0, 0), (0, 0))
    kk = jnp.concatenate([jnp.pad(kb, pad5)[:, :-1], kb], axis=2)
    vv = jnp.concatenate([jnp.pad(vb, pad5)[:, :-1], vb], axis=2)
    pb = positions.reshape(B, nb, BLOCK)
    pk = jnp.concatenate([jnp.pad(pb, ((0, 0), (1, 0), (0, 0)))[:, :-1], pb], axis=2)

    scale = HEAD_DIM_A ** -0.5
    s = jnp.einsum('bnqkgd,bnskd->bnkgqs', qb, kk).astype(jnp.float32) * scale
    dist = (pb[:, :, :, None] - pk[:, :, None, :]).astype(jnp.float32)
    slopes = alibi_slopes(N_HEADS_A).reshape(N_KV_HEADS_A, GROUP_A)
    s = s - slopes[None, None, :, :, None, None] * dist[:, :, None, None]

    qi = jnp.arange(BLOCK)[:, None] + BLOCK
    ki = jnp.arange(2 * BLOCK)[None, :]
    diff = qi - ki
    band = (diff >= 0) & (diff < WINDOW)
    has_prev = (jnp.arange(nb)[:, None, None] > 0) | (ki[None] >= BLOCK)
    valid = band[None] & has_prev
    s = jnp.where(valid[None, :, None, None], s, NEG)

    sink = sinks.astype(jnp.float32).reshape(N_KV_HEADS_A, GROUP_A)
    sink = jnp.broadcast_to(sink[None, None, :, :, None, None], s.shape[:-1] + (1,))
    p = jax.nn.softmax(jnp.concatenate([s, sink], axis=-1), axis=-1)[..., :-1]
    o = jnp.einsum('bnkgqs,bnskd->bnqkgd', p.astype(vv.dtype), vv)
    return o.reshape(B, S, WIDTH_A)

def mla_attention(c_q, c_kv, k_rope, cos, sin, q_lora_norm, w_uq, kv_lora_norm, w_ukv, q_gain, k_gain):
    B, S = c_q.shape[0], c_q.shape[1]
    nb = S // BLOCK
    q = (rms_norm(c_q, q_lora_norm) @ w_uq).reshape(B, S, N_HEADS_B, QK_DIM_B)
    kv = (rms_norm(c_kv, kv_lora_norm) @ w_ukv).reshape(B, S, N_HEADS_B, QK_NOPE_DIM + V_DIM_B)
    k_nope, v = kv[..., :QK_NOPE_DIM], kv[..., QK_NOPE_DIM:]
    k_r = jnp.broadcast_to(k_rope[:, :, None, :], (B, S, N_HEADS_B, QK_ROPE_DIM))
    k = jnp.concatenate([k_nope, k_r], axis=-1)
    q = rms_norm(q, q_gain)
    k = rms_norm(k, k_gain)
    q = jnp.concatenate([q[..., :QK_NOPE_DIM], apply_rope(q[..., QK_NOPE_DIM:], cos, sin)], axis=-1)
    k = jnp.concatenate([k[..., :QK_NOPE_DIM], apply_rope(k[..., QK_NOPE_DIM:], cos, sin)], axis=-1)

    scale = QK_DIM_B ** -0.5
    key_idx = jnp.arange(S)
    qb = jnp.moveaxis(q.reshape(B, nb, BLOCK, N_HEADS_B, QK_DIM_B), 1, 0)

    def one_block(args):
        q_blk, i = args
        s = jnp.einsum('bqhd,bshd->bhqs', q_blk, k).astype(jnp.float32) * scale
        t = i * BLOCK + jnp.arange(BLOCK)
        s = jnp.where(t[:, None] >= key_idx[None, :], s, NEG)
        p = jax.nn.softmax(s, axis=-1)
        return jnp.einsum('bhqs,bshd->bqhd', p.astype(v.dtype), v)

    o = lax.map(one_block, (qb, jnp.arange(nb)))
    return jnp.moveaxis(o, 0, 1).reshape(B, S, WIDTH_B)

def setup_inputs(seed: int = 0) -> dict:
    key = jax.random.key(seed)
    ks = iter(jax.random.split(key, 32))
    L = DEPTH

    def w(shape, fan_in):
        return jax.random.normal(next(ks), shape, jnp.float32) * fan_in ** -0.5

    def gain(shape):
        return 1.0 + 0.02 * jax.random.normal(next(ks), shape, jnp.float32)

    x = jax.random.normal(next(ks), (BATCH, SEQ, D_MODEL), jnp.float32)
    start = jax.random.randint(next(ks), (BATCH, 1), 0, 4096, dtype=jnp.int32)
    positions = start + jnp.arange(SEQ, dtype=jnp.int32)[None, :]
    return {
        "x": x,
        "positions": positions,
        "ffn1_norm": gain((L, D_MODEL)),
        "ffn1_w_gate": w((L, D_MODEL, D_FF), D_MODEL),
        "ffn1_w_up": w((L, D_MODEL, D_FF), D_MODEL),
        "ffn1_w_down": w((L, D_FF, D_MODEL), D_FF),
        "mix_norm": gain((L, D_MODEL)),
        "w_in": w((L, D_MODEL, IN_WIDTH), D_MODEL),
        "swa_q_norm": gain((L, HEAD_DIM_A)),
        "swa_k_norm": gain((L, HEAD_DIM_A)),
        "swa_sinks": 0.5 * jax.random.normal(next(ks), (L, N_HEADS_A), jnp.float32),
        "mla_q_lora_norm": gain((L, Q_LORA_RANK)),
        "mla_w_uq": w((L, Q_LORA_RANK, N_HEADS_B * QK_DIM_B), Q_LORA_RANK),
        "mla_kv_lora_norm": gain((L, KV_LORA_RANK)),
        "mla_w_ukv": w((L, KV_LORA_RANK, N_HEADS_B * (QK_NOPE_DIM + V_DIM_B)), KV_LORA_RANK),
        "mla_q_norm": gain((L, QK_DIM_B)),
        "mla_k_norm": gain((L, QK_DIM_B)),
        "w_branch_a": w((L, WIDTH_A, D_MODEL), WIDTH_A),
        "w_branch_b": w((L, WIDTH_B, D_MODEL), WIDTH_B),
        "w_out": w((L, D_MODEL, D_MODEL), D_MODEL),
        "ffn2_norm": gain((L, D_MODEL)),
        "ffn2_w_gate": w((L, D_MODEL, D_FF), D_MODEL),
        "ffn2_w_up": w((L, D_MODEL, D_FF), D_MODEL),
        "ffn2_w_down": w((L, D_FF, D_MODEL), D_FF),
    }

def reference(x, positions, ffn1_norm, ffn1_w_gate, ffn1_w_up, ffn1_w_down, mix_norm, w_in,
              swa_q_norm, swa_k_norm, swa_sinks, mla_q_lora_norm, mla_w_uq, mla_kv_lora_norm,
              mla_w_ukv, mla_q_norm, mla_k_norm, w_branch_a, w_branch_b, w_out,
              ffn2_norm, ffn2_w_gate, ffn2_w_up, ffn2_w_down):
    B, S, _ = x.shape
    half = QK_ROPE_DIM // 2
    inv_freq = ROPE_BASE ** (-jnp.arange(half, dtype=jnp.float32) / half)
    ang = positions.astype(jnp.float32)[..., None] * inv_freq
    cos = jnp.cos(ang)[:, :, None, :].astype(x.dtype)
    sin = jnp.sin(ang)[:, :, None, :].astype(x.dtype)
    k_rope_cos, k_rope_sin = cos[:, :, 0], sin[:, :, 0]

    for l in range(DEPTH):
        x = x + 0.5 * swiglu(rms_norm(x, ffn1_norm[l]), ffn1_w_gate[l], ffn1_w_up[l], ffn1_w_down[l])

        h = rms_norm(x, mix_norm[l])
        proj = h @ w_in[l]
        qa, ka, va, c_q, c_kv, k_r, g_a, g_b = jnp.split(proj, IN_OFFSETS, axis=-1)
        qa = qa.reshape(B, S, N_HEADS_A, HEAD_DIM_A)
        ka = ka.reshape(B, S, N_KV_HEADS_A, HEAD_DIM_A)
        va = va.reshape(B, S, N_KV_HEADS_A, HEAD_DIM_A)
        o_a = swa_attention(qa, ka, va, positions, swa_q_norm[l], swa_k_norm[l], swa_sinks[l])
        o_b = mla_attention(c_q, c_kv, k_r, cos, sin, mla_q_lora_norm[l], mla_w_uq[l],
                            mla_kv_lora_norm[l], mla_w_ukv[l], mla_q_norm[l], mla_k_norm[l])
        merged = jax.nn.sigmoid(g_a) * (o_a @ w_branch_a[l]) + jax.nn.sigmoid(g_b) * (o_b @ w_branch_b[l])
        x = x + merged @ w_out[l]

        x = x + 0.5 * swiglu(rms_norm(x, ffn2_norm[l]), ffn2_w_gate[l], ffn2_w_up[l], ffn2_w_down[l])
    return x


_drawn_inputs = setup_inputs


def setup_inputs(seed=0):
    import zlib

    import numpy as np

    out = dict(_drawn_inputs(seed))
    spreads = {}
    factors = {'ffn1_norm': 4.458,
     'mix_norm': 6.258,
     'swa_q_norm': 8.0,
     'swa_k_norm': 8.0,
     'swa_sinks': 22.968,
     'mla_q_lora_norm': 8.0,
     'mla_kv_lora_norm': 8.0,
     'mla_q_norm': 8.0,
     'mla_k_norm': 8.0,
     'ffn2_norm': 5.159}
    for name, (base, spread) in spreads.items():
        noise = np.random.default_rng([zlib.crc32(name.encode()), seed]).standard_normal(out[name].shape)
        drawn = base * np.exp(spread * noise) if base else spread * noise
        out[name] = __import__('jax').numpy.asarray(drawn.astype(out[name].dtype))
    for name, factor in factors.items():
        out[name] = (out[name] * factor).astype(out[name].dtype)
    return out
```

```python
from contextlib import ExitStack

import numpy as np

import concourse.bass as bass
from concourse import mybir

F32 = mybir.dt.float32
F32R = mybir.dt.float32r
I32 = mybir.dt.int32
ALU = mybir.AluOpType
ACT = mybir.ActivationFunctionType
AX = mybir.AxisListType.X

P = 128
D_MODEL, SEQ, DEPTH, D_FF = 1024, 256, 2, 2816
TT = SEQ // P
KC = D_MODEL // P
HALF = 512
HA, DA, GA = 8, 64, 4
HB, NOPE, ROPE, VB = 8, 64, 32, 64
QKB = NOPE + ROPE
QRANK, KVRANK = 256, 128
EPS = 1e-6
NEG = -1e30
SCALE_A = DA ** -0.5
SCALE_B = float(np.float32(QKB ** -0.5))

FB = D_FF // P
GU_COLS = 2 * KC * P
DN_COLS = D_MODEL
PROJ_COLS = 512 + 128 + 128 + QRANK + KVRANK + ROPE
Q0, K0, V0, CQ0, CKV0, KR0 = 0, 512, 640, 768, 1024, 1152
UQ_COLS = QRANK // P * HB * QKB
UKV_COLS = HB * (NOPE + VB)
MIX = ([("proj", k) for k in range(KC)] + [("gate", j) for j in range(4)] + [("ukv", 0), ("uq", 0)]
       + [("gate", j) for j in range(4, KC)] + [("branch", j) for j in range(4)] + [("out", j) for j in range(4)])
UKV, UQ, GATE4, BRANCH, OUT = KC + 4, KC + 5, KC + 6, KC + 10, KC + 14
MIX_SLOTS = 3
MIX_COLS = {"proj": PROJ_COLS, "gate": GU_COLS, "uq": UQ_COLS, "ukv": UKV_COLS, "branch": GU_COLS, "out": GU_COLS}
MIX0 = FB
FFN2_0 = FB + len(MIX)
BLOCKS = 2 * FB + len(MIX)


def at_block(kind, j):
    return MIX0 + MIX.index((kind, j))


assert FB % 2 == 0 and BLOCKS % 2 == 0 and FFN2_0 % 2 == 0

GATE_BANK = (1, 2, 1, 2, 3, 2, 3, 2)
LATENT_BANK = (4, 5, 6, 7, 0, 1, 3, 4)

ROOT_STEPS = 9
RSQRT_SEED = float(0x5f3759df)

TWO_PI = 2 * np.pi
TWO_PI_PARTS = (6.28125, float(np.float32(TWO_PI - 6.28125) // 2 ** -20 * 2 ** -20), 0.0)
TWO_PI_PARTS = TWO_PI_PARTS[:2] + (float(np.float32(TWO_PI - TWO_PI_PARTS[0] - TWO_PI_PARTS[1])),)
HALF_PI = float(np.float32(np.pi / 2))
PI_IN = 3.1415925
ROUND = 1.5 * 2.0 ** 23
TAB_STEPS = 7 + 2 * 11

V_STEPS = 29
SEGS = 3


class Signal:

    def __init__(self, sem, per_layer, first=0):
        self.sem, self.per_layer, self.first = sem, per_layer, first

    def at(self, layer, k):
        return layer * self.per_layer + (k + 1 + self.first)


def build(nc, x_in, pos_in, cols_in, rows_in, w_ffn, w_proj, w_gate, w_uq, w_ukv, w_branch, w_out,
          masks_in, freq_in, out):
    with ExitStack() as ctx:
        def sb(name, shape, dt=F32):
            return ctx.enter_context(nc.sbuf_tensor(name, shape, dt))

        def signal(name, per_layer, first=0):
            return Signal(ctx.enter_context(nc.semaphore(name)), per_layer, first)

        w_raw = sb("w_raw", [P, MIX_SLOTS * GU_COLS])
        w_hi = sb("w_hi", [P, MIX_SLOTS * GU_COLS], F32R)
        w_lo = sb("w_lo", [P, MIX_SLOTS * GU_COLS], F32R)
        raw = [w_raw[:, i * (GU_COLS + DN_COLS):(i + 1) * (GU_COLS + DN_COLS)] for i in range(2)]
        wh_gu, wl_gu = ([w[:, i * GU_COLS:(i + 1) * GU_COLS] for i in range(2)] for w in (w_hi, w_lo))
        wh_d, wl_d = ([w[:, 2 * GU_COLS + i * DN_COLS:2 * GU_COLS + (i + 1) * DN_COLS] for i in range(2)]
                      for w in (w_hi, w_lo))
        mix_raw, mix_hi, mix_lo = ([w[:, i * GU_COLS:(i + 1) * GU_COLS] for i in range(MIX_SLOTS)]
                                   for w in (w_raw, w_hi, w_lo))
        x = sb("x", [P, TT, D_MODEL])
        hTh = sb("hTh", [P, KC, SEQ], F32R)
        hTl = sb("hTl", [P, KC, SEQ], F32R)
        aTh = sb("aTh", [P, 2, SEQ], F32R)
        aTl = sb("aTl", [P, 2, SEQ], F32R)
        work = sb("work", [P, 4 * SEQ])
        silu = work[:, 0:2 * SEQ].rearrange("p (b n) -> p b n", b=2)
        prod = work[:, 2 * SEQ:].rearrange("p (b n) -> p b n", b=2)
        vB = work[:, :].rearrange("p (t n) -> p t n", t=TT)
        merge = work[:, :].rearrange("p (b n) -> p b n", b=2)
        proj = sb("proj", [P, TT, PROJ_COLS])
        sq = sb("sq", [P, TT * HB * QKB])
        qTA = sb("qTA", [P, 4, SEQ])
        kTA = sb("kTA", [P, SEQ])
        diag = kTA[:, :].rearrange("p (t n) -> p t n", t=TT)
        qkB_PT = sb("qkB_PT", [P, 2 * TT * HB * QKB])
        qB = qkB_PT[:, 0:TT * HB * QKB].rearrange("p (t n) -> p t n", t=TT)
        kB = qkB_PT[:, TT * HB * QKB:].rearrange("p (t n) -> p t n", t=TT)
        PT = qkB_PT[:, :].rearrange("p (h n) -> p h n", h=HB)
        qTB = sb("qTB", [QKB, HB, SEQ])
        kTB = sb("kTB", [QKB, HB, SEQ])
        S = sb("S", [P, HB, SEGS * P])
        O = sq[:, 0:TT * HB * VB].rearrange("p (t n) -> p t n", t=TT)
        oTh = sb("oTh", [P, 8, SEQ], F32R)
        oTl = sb("oTl", [P, 8, SEQ], F32R)
        SG = sb("SG", [P, KC, 2 * SEQ])
        ident = sb("ident", [P, P])
        maskA = sb("maskA", [P, SEGS * P])
        maskB = sb("maskB", [P, SEGS * P])
        negdist = maskA
        posk_i = sb("posk_i", [P, SEQ], I32)
        posk = S[:, 0, 0:SEQ]
        posq_i = sb("posq_i", [P, TT], I32)
        posq = sb("posq", [P, TT])
        turn = sb("turn", [P, 2, TT * 16])
        trig = sb("trig", [P, 2, TT, 16])
        cols = sb("cols", [P, 7 + 3 * KC])
        rows = sb("rows", [P, 2 * ROPE + HA])
        cg = sb("cg", [P, 2, TT, ROPE])
        sg = sb("sg", [P, 2, TT, ROPE])
        krr = sb("krr", [P, TT, ROPE])
        krt = sb("krt", [P, 2, TT, ROPE])
        minus_half = sb("minus_half", [P, TT * HA + 4])
        small = sb("small", [P, 272])
        ss = sb("ss", [P, 2 * TT])
        root = sb("root", [P, 7, TT])
        ssC, varC, rsC = small[:, 6:12], small[:, 12:16], small[:, 16:20]
        ssA, varA, rsA = small[:, 20:40], small[:, 40:60], small[:, 60:80]
        ssQ, varQ, rsQ = small[:, 80:96], small[:, 96:112], small[:, 112:128]
        ssK, varK, rsK, ssR = small[:, 128:144], small[:, 144:160], small[:, 160:176], small[:, 176:178]
        mx = small[:, 178:202]
        top, ntop, den, sinkx = small[:, 202:218], small[:, 218:234], small[:, 234:250], small[:, 250:266]
        esink, rden2 = sb("esink", [P, 16]), sb("rden2", [P, 2, 16])
        sink8 = sb("sink8", [P, HA])
        dist = S[:, 1, :]
        ang = S[:, 2, 0:7 * TT * 16].rearrange("p (s n) -> p s n", s=7)
        freq = sb("freq", [P, 16])

        ps = ctx.enter_context(nc.psum_tensor("ps", [P, 8, HALF], F32))

        raw_in = [signal(f"raw_in{i}", 16 * FB) for i in range(2)]
        mix_in = [signal(f"mix_in{i}", 16 * len(range(i, len(MIX), MIX_SLOTS))) for i in range(MIX_SLOTS)]
        gu_used = signal("gu_used", BLOCKS, 2)
        d_used = signal("d_used", 2 * FB, 2)
        hi_gu = signal("hi_gu", BLOCKS)
        lo_gu = signal("lo_gu", BLOCKS, 2)
        hi_d = signal("hi_d", 2 * FB)
        lo_d = signal("lo_d", 2 * FB, 2)
        x_done = signal("x_done", 6 * TT, 2 * TT)
        ss_done = signal("ss_done", 6 * TT)
        root_step = signal("root_step", 3 * ROOT_STEPS)
        diag_done = signal("diag_done", 3 * TT)
        ht_ps = signal("ht_ps", 12)
        ht_hi = signal("ht_hi", 12)
        ht_lo = signal("ht_lo", 12)
        silu_done = signal("silu_done", 2 * FB)
        prod_done = signal("prod_done", 2 * FB, 2)
        a_hi = signal("a_hi", 2 * FB)
        a_lo = signal("a_lo", 2 * FB)
        acc_done = signal("acc_done", 3 * 3)
        small_in = signal("small_in", 2 * 16)
        x_in_done = signal("x_in_done", 0)
        ident_in = signal("ident_in", 0)
        table_in = signal("table_in", 0)
        tab = signal("tab", 0)
        trig_done = signal("trig_done", 1)
        half_set = signal("half_set", 0)
        silu_ready = signal("silu_ready", 0)
        out_done = signal("out_done", 0)

        proj_act = signal("proj_act", 4)
        proj_dve = signal("proj_dve", 1)
        tanh_done = signal("tanh_done", KC)
        v = signal("v", V_STEPS)
        c_var = signal("c_var", 2)
        c_rs = signal("c_rs", 1)
        c_norm = signal("c_norm", 1)
        c_ps = signal("c_ps", 2)
        c_hi = signal("c_hi", 2)
        c_lo = signal("c_lo", 2)
        a_var = signal("a_var", 1)
        a_rs = signal("a_rs", 1)
        a_norm = signal("a_norm", 1)
        a_ps = signal("a_ps", 1)
        a_T = signal("a_T", 3)
        q_sq = signal("q_sq", 1)
        q_ss = signal("q_ss", 1)
        q_var = signal("q_var", 1)
        q_rs = signal("q_rs", 1)
        q_rot = signal("q_rot", 1)
        k_sq = signal("k_sq", 1)
        k_var = signal("k_var", 1)
        k_rs = signal("k_rs", 1)
        k_norm = signal("k_norm", 1)
        v_copied = signal("v_copied", 2)
        b_ps = signal("b_ps", 8)
        bq_T = signal("bq_T", 4)
        bk_T = signal("bk_T", 4)
        s_ps = signal("s_ps", 2 * HB)
        s_sb = signal("s_sb", 2 * HB)
        top_done = signal("top_done", 4)
        p_done = signal("p_done", 2 * HB)
        sink_in = signal("sink_in", 1)
        sink_out = signal("sink_out", 1)
        rden_done = signal("rden_done", 2)
        pt_ps = signal("pt_ps", 2 * HB)
        pt_act = signal("pt_act", HB)
        pt_dve = signal("pt_dve", HB)

        def pt_copied(l, br, h):
            sig = (pt_act, pt_dve)[(br + h // 4) % 2]
            return sig.sem, sig.at(l, br * 4 + h % 4)

        o_ps = signal("o_ps", 2 * TT)
        o_done = signal("o_done", 2 * TT)
        ot_ps = signal("ot_ps", 4)
        ot_hi = signal("ot_hi", 4)
        ot_lo = signal("ot_lo", 4)
        br_ps = signal("br_ps", 4)
        gated_a = signal("gated_a", KC // 2)
        gated_b = signal("gated_b", KC // 2)
        merged = signal("merged", KC // 2)
        m_hi = signal("m_hi", KC // 2)
        m_lo = signal("m_lo", KC // 2)

        block = ctx.enter_context(nc.Block())

        @block.sync
        def _(sp):
            sp.dma_start(ident[:, :], masks_in[0, :, 0:P]).then_inc(ident_in.sem, 16)
            sp.dma_start(x[:, :, :], x_in.rearrange("b (t p) d -> p (b t) d", p=P)).then_inc(x_in_done.sem, 16)

            with sp.Fori(0, DEPTH) as l:
                def load_mix(k):
                    kind, j = MIX[k]
                    src = {"proj": w_proj, "gate": w_gate, "uq": w_uq, "ukv": w_ukv,
                           "branch": w_branch, "out": w_out}[kind]
                    count = sum(1 for other, _ in MIX if other == kind)
                    row = sp.snap(l * count + j)
                    if k < MIX_SLOTS:
                        sp.wait_ge(lo_d.sem, lo_d.at(l, FB - 2 + min(k, 1)))
                    else:
                        sp.wait_ge(lo_gu.sem, lo_gu.at(l, MIX0 + k - MIX_SLOTS))
                    sp.dma_start(mix_raw[k % MIX_SLOTS][:, 0:MIX_COLS[kind]], src[row])\
                      .then_inc(mix_in[k % MIX_SLOTS].sem, 16)

                def load_small(row):
                    sp.dma_start(cols[:, :], cols_in[row]).then_inc(small_in.sem, 16)
                    sp.dma_start(rows[:, :], rows_in[bass.ds(row, 1), :].to_broadcast([P, 2 * ROPE + HA]))\
                      .then_inc(small_in.sem, 16)

                def load_ffn(w, first):
                    with sp.Fori(0, (FB - first) // 2) as i:
                        for b in range(2):
                            row = sp.snap(l * (2 * FB) + i * 2 + (w * FB + b + first))
                            sp.wait_ge(lo_d.sem, l * (2 * FB) + i * 2 + (w * FB + b + first + 1))
                            sp.dma_start(raw[b], w_ffn[row]).then_inc(raw_in[b].sem, 16)

                load_ffn(0, 0)
                for k in range(len(MIX)):
                    load_mix(k)
                for b in range(2):
                    row = sp.snap(l * (2 * FB) + (FB + b))
                    if b == 0:
                        sp.wait_ge(lo_gu.sem, lo_gu.at(l, FFN2_0 - 1))
                    sp.dma_start(raw[b], w_ffn[row]).then_inc(raw_in[b].sem, 16)
                load_ffn(1, 2)
                row = sp.snap(l + 1)
                sp.wait_ge(ht_lo.sem, ht_lo.at(l, 11))
                load_small(row)
            for i in range(2 * TT):
                t, half = i // 2, slice(i % 2 * HALF, (i % 2 + 1) * HALF)
                sp.wait_ge(x_done.sem, x_done.at(DEPTH - 1, 4 * TT + i))
                sp.dma_start(out[0, t * P:(t + 1) * P, half], x[:, t, half]).then_inc(out_done.sem, 16)
            sp.wait_ge(out_done.sem, 16 * 2 * TT)
            sp.wait_ge(small_in.sem, small_in.per_layer * (DEPTH + 1))

        @block.gpsimd
        def _(pool):
            for s in (gu_used, d_used, lo_gu, lo_d, prod_done):
                pool.sem_inc(s.sem, s.first)
            pool.memset(minus_half[:, :], -0.5).then_inc(half_set.sem, 1)
            pool.wait_ge(half_set.sem, 1)
            pool.wait_ge(x_in_done.sem, 16)
            pool.sem_inc(x_done.sem, x_done.first)

            pool.dma_start(maskA[:, :], masks_in[1]).then_inc(table_in.sem, 16)
            pool.dma_start(maskB[:, :], masks_in[2]).then_inc(table_in.sem, 16)
            pool.dma_start(freq[:, :], freq_in).then_inc(table_in.sem, 16)
            pool.dma_start(posk_i[:, :], pos_in.to_broadcast([P, SEQ])).then_inc(table_in.sem, 16)
            with nc.allow_non_contiguous_dma(reason="256 positions, once"):
                pool.dma_start(posq_i[:, :], pos_in.rearrange("b (t p) -> p (b t)", p=P)).then_inc(table_in.sem, 16)
            step = [0]

            def then(ins):
                step[0] += 1
                ins.then_inc(tab.sem, 1)
                pool.wait_ge(tab.sem, step[0])

            pool.wait_ge(table_in.sem, 16 * 5)
            then(pool.tensor_copy(posk, posk_i[:, :]))
            then(pool.tensor_copy(posq[:, :], posq_i[:, :]))
            for t, (a, b) in enumerate(((0, P), (P, SEGS * P))):
                then(pool.tensor_scalar(dist[:, a:b], posk[:, 0:b - a], posq[:, t:t + 1], None, ALU.subtract))
            then(pool.tensor_tensor(negdist[:, :], maskA[:, :], dist[:, 0:SEGS * P], ALU.add))
            for t in range(TT):
                then(pool.tensor_scalar(ang[:, 0, t * 16:(t + 1) * 16], freq[:, :], posq[:, t:t + 1], None, ALU.mult))
            angle = ang[:, 0, :]
            for q, shift in ((0, 0.25), (1, 0.0)):
                then(pool.tensor_scalar(ang[:, 1, :], angle, 1.0 / TWO_PI, shift, ALU.mult, ALU.add))
                then(pool.tensor_scalar(ang[:, 2, :], ang[:, 1, :], ROUND, None, ALU.add))
                then(pool.tensor_scalar(ang[:, 3, :], ang[:, 2, :], ROUND, None, ALU.subtract))
                rest = angle
                for i, part in enumerate(TWO_PI_PARTS):
                    then(pool.tensor_scalar(ang[:, 6, :], ang[:, 3, :], -part, None, ALU.mult))
                    then(pool.tensor_tensor(ang[:, 4 + i % 2, :], ang[:, 6, :], rest, ALU.add))
                    rest = ang[:, 4 + i % 2, :]
                then(pool.tensor_scalar(ang[:, 5, :], rest, HALF_PI if q == 0 else 0.0, PI_IN, ALU.add, ALU.min))
                then(pool.tensor_scalar(turn[:, q, :], ang[:, 5, :], -PI_IN, None, ALU.max))
            assert step[0] == TAB_STEPS

            with pool.Fori(0, DEPTH) as l:
                for vec, to, ready, done in ((varC, rsC, c_var, c_rs), (varA, rsA, a_var, a_rs),
                                             (varQ, rsQ, q_var, q_rs), (varK, rsK, k_var, k_rs)):
                    pool.wait_ge(ready.sem, ready.at(l, ready.per_layer - 1))
                    pool.tensor_tensor(to, vec, minus_half[:, 0:vec.shape[1]], ALU.pow).then_inc(done.sem, 1)

        @block.scalar
        def _(act):
            act.dma_start(cols[:, :], cols_in[0]).then_inc(small_in.sem, 16)
            act.dma_start(rows[:, :], rows_in[0:1, :].to_broadcast([P, 2 * ROPE + HA])).then_inc(small_in.sem, 16)
            act.wait_ge(half_set.sem, 1)
            act.activation(esink[:, 0:1], minus_half[:, 0:1], ACT.Silu).then_inc(silu_ready.sem, 1)
            act.wait_ge(silu_ready.sem, 1)

            with act.Fori(0, DEPTH) as l:
                def split_mix(k):
                    m, ncols = k % MIX_SLOTS, MIX_COLS[MIX[k][0]]
                    act.wait_ge(mix_in[m].sem, l * mix_in[m].per_layer + 16 * (k // MIX_SLOTS + 1))
                    if k < 2:
                        act.wait_ge(gu_used.sem, gu_used.at(l, MIX0 + k - 2))
                    elif k == 2:
                        act.wait_ge(d_used.sem, d_used.at(l, FB - 1))
                    else:
                        act.wait_ge(gu_used.sem, gu_used.at(l, MIX0 + k - MIX_SLOTS))
                    act.activation(mix_hi[m][:, 0:ncols], mix_raw[m][:, 0:ncols], ACT.Copy).then_inc(hi_gu.sem, 1)

                def split_gu(i2, o, e, b):
                    act.wait_ge(raw_in[b].sem, l * (16 * FB) + i2 * 8 + 16 * (e // 2 + 1))
                    act.wait_ge(gu_used.sem, l * BLOCKS + i2 + (o + 1))
                    act.activation(wh_gu[b], raw[b][:, 0:GU_COLS], ACT.Copy).then_inc(hi_gu.sem, 1)

                def split_d(i2, e, b):
                    act.wait_ge(d_used.sem, l * (2 * FB) + i2 + (e + 1))
                    act.activation(wh_d[b], raw[b][:, GU_COLS:], ACT.Copy).then_inc(hi_d.sem, 1)

                def swiglu(i2, o, e, b):
                    act.wait_ge(gu_used.sem, l * BLOCKS + i2 + (o + 3))
                    act.activation(silu[:, b, :], ps[:, b, 0:SEQ], ACT.Silu).then_inc(silu_done.sem, 1)
                    act.wait_ge(prod_done.sem, l * (2 * FB) + i2 + (e + 3))
                    act.activation(aTh[:, b, :], prod[:, b, :], ACT.Copy).then_inc(a_hi.sem, 1)

                def norm(n, split_next):
                    for t in range(TT):
                        for h in range(2):
                            act.wait_ge(x_done.sem, l * (6 * TT) + (4 * n + 2 * t + h + 1))
                            act.activation(SG[:, 2 * t + h, :], x[:, t, h * HALF:(h + 1) * HALF], ACT.Square,
                                           accum_out=ss[:, 2 * t + h:2 * t + h + 1]).then_inc(ss_done.sem, 1)
                    split_next()
                    act.wait_ge(small_in.sem, small_in.per_layer * (l + 1))
                    for c in range(KC):
                        if c % 2 == 0:
                            act.wait_ge(ht_ps.sem, ht_ps.at(l, 4 * n + c // 2))
                        ins = act.activation(hTh[:, c, :], ps[:, c // 2, (c % 2) * SEQ:(c % 2 + 1) * SEQ], ACT.Copy,
                                             scale=cols[:, 7 + n * KC + c:8 + n * KC + c])
                        if c % 2:
                            ins.then_inc(ht_hi.sem, 1)

                def ffn(w, o0):
                    e0 = w * FB
                    norm(2 * w, lambda: split_gu(0, o0, e0, 0))
                    split_d(0, e0, 0)
                    split_gu(0, o0 + 1, e0 + 1, 1)
                    swiglu(0, o0, e0, 0)
                    split_d(0, e0 + 1, 1)
                    with act.Fori(0, FB // 2 - 1) as i:
                        for b in range(2):
                            split_gu(i * 2, o0 + 2 + b, e0 + 2 + b, b)
                            swiglu(i * 2, o0 + 1 + b, e0 + 1 + b, 1 - b)
                            split_d(i * 2, e0 + 2 + b, b)
                    swiglu(0, o0 + FB - 1, e0 + FB - 1, 1)

                ffn(0, 0)
                norm(1, lambda: split_mix(0))
                for k in range(1, KC + 2):
                    split_mix(k)
                    if k == KC // 2:
                        act.wait_ge(tab.sem, TAB_STEPS)
                        act.activation(trig[:, :, :, :].rearrange("p q t f -> p q (t f)"), turn[:, :, :], ACT.Sin)\
                           .then_inc(trig_done.sem, 1)
                act.wait_ge(gu_used.sem, gu_used.at(l, at_block("proj", KC - 1)))
                for t in range(TT):
                    act.activation(proj[:, t, HALF:2 * HALF], ps[:, 5 + 2 * t, :], ACT.Copy).then_inc(proj_act.sem, 1)
                for t in range(TT):
                    act.activation(proj[:, t, 0:HALF], ps[:, 4 + 2 * t, :], ACT.Copy).then_inc(proj_act.sem, 1)

                def gate_tanh(j):
                    act.wait_ge(gu_used.sem, gu_used.at(l, at_block("gate", j)))
                    act.activation(SG[:, j, :], ps[:, GATE_BANK[j], :], ACT.Tanh, scale=0.5).then_inc(tanh_done.sem, 1)

                split_mix(KC + 2)
                gate_tanh(0)
                split_mix(KC + 3)
                for c in range(3):
                    if c != 1:
                        act.wait_ge(c_ps.sem, c_ps.at(l, c // 2))
                    src = ps[:, 3, c * SEQ:(c + 1) * SEQ] if c < 2 else ps[:, 0, 0:SEQ]
                    ins = act.activation(oTh[:, c, :], src, ACT.Copy, scale=cols[:, c:c + 1])
                    if c != 0:
                        ins.then_inc(c_hi.sem, 1)
                gate_tanh(1)
                split_mix(UKV)
                gate_tanh(2)
                act.wait_ge(a_ps.sem, a_ps.at(l, 0))
                for c in range(2):
                    act.activation(qTA[:, 2 * c:2 * c + 2, :].rearrange("p c n -> p (c n)"), ps[:, 4 + c, :], ACT.Copy,
                                   scale=cols[:, 3:4]).then_inc(a_T.sem, 1)
                act.activation(kTA[:, :], ps[:, 6, 0:SEQ], ACT.Copy, scale=cols[:, 4:5]).then_inc(a_T.sem, 1)
                split_mix(UQ)
                gate_tanh(3)
                split_mix(GATE4)
                act.wait_ge(gu_used.sem, gu_used.at(l, at_block("ukv", 0)))
                act.activation(vB[:, 0, :], ps[:, 3, :], ACT.Copy).then_inc(v_copied.sem, 1)
                act.activation(vB[:, 1, :], ps[:, 2, :], ACT.Copy).then_inc(v_copied.sem, 1)
                split_mix(GATE4 + 1)
                act.wait_ge(gu_used.sem, gu_used.at(l, at_block("uq", 0)))
                act.activation(sq[:, :].rearrange("p (b n) -> p b n", b=4), ps[:, 4:8, 0:HB * QKB // 2], ACT.Square)\
                   .then_inc(q_sq.sem, 1)
                act.wait_ge(q_ss.sem, q_ss.at(l, 0))
                act.activation(sq[:, 0:2 * HALF].rearrange("p (b n) -> p b n", b=2), ps[:, 0:2, :], ACT.Square)\
                   .then_inc(k_sq.sem, 1)
                split_mix(GATE4 + 2)

                def exps(br, heads):
                    for h in heads:
                        act.wait_ge(top_done.sem, top_done.at(l, 2 * br + h // 4))
                        for t, (a, b) in enumerate(((0, P), (P, SEGS * P))):
                            ins = act.activation(S[:, h, a:b], S[:, h, a:b], ACT.Exp, bias=ntop[:, 2 * h + t:2 * h + t + 1],
                                                 scale=(SCALE_A, SCALE_B)[br], accum_out=den[:, 2 * h + t:2 * h + t + 1])
                        ins.then_inc(p_done.sem, 1)

                def copy_pt(br):
                    for h in range(4 * br, 4 * br + 4):
                        act.wait_ge(pt_ps.sem, pt_ps.at(l, br * HB + h))
                        act.activation(PT[:, h, :], ps[:, 4 + h % 4, 0:SEGS * P], ACT.Copy).then_inc(pt_act.sem, 1)

                def o_high(br):
                    for c in range(2):
                        act.wait_ge(ot_ps.sem, ot_ps.at(l, 2 * br + c))
                        act.activation(oTh[:, 4 * br + 2 * c:4 * br + 2 * c + 2, :].rearrange("p c n -> p (c n)"),
                                       ps[:, 4 * br + c, :], ACT.Copy).then_inc(ot_hi.sem, 1)

                gate_tanh(4)
                split_mix(GATE4 + 3)
                exps(0, range(HB))
                act.activation(esink[:, :], sinkx, ACT.Exp).then_inc(sink_out.sem, 1)
                gate_tanh(5)
                gate_tanh(6)
                for f in range(4):
                    act.wait_ge(b_ps.sem, b_ps.at(l, f))
                    act.activation(qTB[:, 2 * f:2 * f + 2, :].rearrange("p h n -> p (h n)"), ps[0:QKB, LATENT_BANK[f], :],
                                   ACT.Copy, scale=cols[0:QKB, 5:6]).then_inc(bq_T.sem, 1)
                split_mix(BRANCH)
                copy_pt(0)
                gate_tanh(7)
                split_mix(BRANCH + 1)
                o_high(0)
                exps(1, range(HB))
                copy_pt(1)
                split_mix(BRANCH + 2)
                split_mix(BRANCH + 3)
                o_high(1)
                split_mix(OUT)
                for p, following in enumerate((OUT + 1, None, OUT + 2, OUT + 3)):
                    act.wait_ge(merged.sem, merged.at(l, p))
                    act.activation(hTh[:, 2 * p:2 * p + 2, :].rearrange("p c n -> p (c n)"), merge[:, p % 2, :], ACT.Copy)\
                       .then_inc(m_hi.sem, 1)
                    if following is not None:
                        split_mix(following)
                ffn(1, FFN2_0)

        @block.vector
        def _(dve):
            dve.wait_ge(ident_in.sem, 16)
            with dve.Fori(0, DEPTH) as l:
                def split_mix(k):
                    m, ncols = k % MIX_SLOTS, MIX_COLS[MIX[k][0]]
                    dve.wait_ge(hi_gu.sem, hi_gu.at(l, MIX0 + k))
                    dve.tensor_tensor(mix_lo[m][:, 0:ncols], mix_raw[m][:, 0:ncols], mix_hi[m][:, 0:ncols].bitcast(F32),
                                      ALU.subtract).then_inc(lo_gu.sem, 1)

                def split_gu(i2, o, b):
                    dve.wait_ge(hi_gu.sem, l * BLOCKS + i2 + (o + 1))
                    dve.tensor_tensor(wl_gu[b], raw[b][:, 0:GU_COLS], wh_gu[b].bitcast(F32), ALU.subtract)\
                       .then_inc(lo_gu.sem, 1)

                def split_d(i2, e, b):
                    dve.wait_ge(hi_d.sem, l * (2 * FB) + i2 + (e + 1))
                    dve.tensor_tensor(wl_d[b], raw[b][:, GU_COLS:], wh_d[b].bitcast(F32), ALU.subtract)\
                       .then_inc(lo_d.sem, 1)

                def swiglu(i2, e, b):
                    dve.wait_ge(silu_done.sem, l * (2 * FB) + i2 + (e + 1))
                    dve.tensor_tensor(prod[:, b, :], silu[:, b, :], ps[:, b, SEQ:2 * SEQ], ALU.mult)\
                       .then_inc(prod_done.sem, 1)
                    dve.wait_ge(a_hi.sem, l * (2 * FB) + i2 + (e + 1))
                    dve.tensor_tensor(aTl[:, b, :], prod[:, b, :], aTh[:, b, :].bitcast(F32), ALU.subtract)\
                       .then_inc(a_lo.sem, 1)

                def residual(n, factor):
                    for t in range(TT):
                        for h in range(2):
                            if 2 * t + h < 3:
                                dve.wait_ge(acc_done.sem, acc_done.at(l, 3 * n + 2 * t + h))
                            elif n == 1:
                                dve.wait_ge(gu_used.sem, gu_used.at(l, FFN2_0 - 1))
                            else:
                                dve.wait_ge(d_used.sem, d_used.at(l, FB * (n // 2 + 1) - 1))
                            part = x[:, t, h * HALF:(h + 1) * HALF]
                            dve.scalar_tensor_tensor(out=part, in0=ps[:, 4 + 2 * t + h, :], scalar=factor, in1=part,
                                                     op0=ALU.mult, op1=ALU.add).then_inc(x_done.sem, 1)

                def inverse_roots(n):
                    v, g, square, a, p, g2, factor = (root[:, i, :] for i in range(7))
                    done = [0]

                    def then(ins):
                        ins.then_inc(root_step.sem, 1)
                        dve.wait_ge(root_step.sem, root_step.at(l, n * ROOT_STEPS + done[0]))
                        done[0] += 1

                    dve.wait_ge(ss_done.sem, ss_done.at(l, 4 * n + 2 * TT - 1))
                    halves = ss[:, :].rearrange("p (t h) -> p t h", h=2)
                    then(dve.scalar_tensor_tensor(out=v, in0=halves[:, :, 0], scalar=D_MODEL * EPS, in1=halves[:, :, 1],
                                                  op0=ALU.add, op1=ALU.add))
                    then(dve.tensor_scalar(g.bitcast(I32), v.bitcast(I32), -0.5, RSQRT_SEED, ALU.mult, ALU.add))
                    then(dve.tensor_tensor(square, g, g, ALU.mult))
                    then(dve.tensor_tensor(a, square, v, ALU.mult))
                    then(dve.scalar_tensor_tensor(out=p, in0=a, scalar=-10.0 / 3.0, in1=a, op0=ALU.add, op1=ALU.mult))
                    then(dve.scalar_tensor_tensor(out=g2, in0=p, scalar=5.0, in1=g, op0=ALU.add, op1=ALU.mult))
                    then(dve.tensor_tensor(square, g2, g2, ALU.mult))
                    then(dve.tensor_tensor(a, square, v, ALU.mult))
                    unit, root_d = 3.0 / 8.0, D_MODEL ** 0.5
                    then(dve.tensor_scalar(factor, a, -0.5 * unit ** 3 * root_d, 1.5 * unit * root_d, ALU.mult, ALU.add))
                    assert done[0] == ROOT_STEPS
                    for t in range(TT):
                        dve.tensor_scalar(diag[:, t, :], ident[:, :], g2[:, t:t + 1], factor[:, t:t + 1], ALU.mult,
                                          ALU.mult).then_inc(diag_done.sem, 1)

                def norm(n, split_next):
                    inverse_roots(n)
                    split_next()
                    dve.wait_ge(small_in.sem, small_in.per_layer * (l + 1))
                    for c in range(KC):
                        if c % 2 == 0:
                            dve.wait_ge(ht_hi.sem, ht_hi.at(l, 4 * n + c // 2))
                        ins = dve.scalar_tensor_tensor(out=hTl[:, c, :], in0=ps[:, c // 2, (c % 2) * SEQ:(c % 2 + 1) * SEQ],
                                                 scalar=cols[:, 7 + n * KC + c:8 + n * KC + c],
                                                 in1=hTh[:, c, :].bitcast(F32), op0=ALU.mult, op1=ALU.subtract)
                        if c % 2:
                            ins.then_inc(ht_lo.sem, 1)

                def ffn(w, o0):
                    e0 = w * FB
                    if w == 1:
                        residual(1, 0.5)
                    norm(2 * w, lambda: split_gu(0, o0, 0))
                    split_d(0, e0, 0)
                    split_gu(0, o0 + 1, 1)
                    swiglu(0, e0, 0)
                    split_d(0, e0 + 1, 1)
                    with dve.Fori(0, FB // 2 - 1) as i:
                        for b in range(2):
                            split_gu(i * 2, o0 + 2 + b, b)
                            swiglu(i * 2, e0 + 1 + b, 1 - b)
                            split_d(i * 2, e0 + 2 + b, b)
                    swiglu(0, e0 + FB - 1, 1)

                ffn(0, 0)
                residual(0, 0.5)
                chain = [0]

                def then(ins):
                    ins.then_inc(v.sem, 1)
                    dve.wait_ge(v.sem, v.at(l, chain[0]))
                    chain[0] += 1

                norm(1, lambda: split_mix(0))
                for k in range(1, KC + 2):
                    split_mix(k)
                dve.wait_ge(gu_used.sem, gu_used.at(l, at_block("proj", KC - 1)))
                dve.tensor_copy(proj[:, :, CKV0:PROJ_COLS],
                                ps[:, 0, 0:2 * (KVRANK + ROPE)].rearrange("p (t n) -> p t n", t=TT))\
                   .then_inc(proj_dve.sem, 1)
                dve.wait_ge(proj_dve.sem, proj_dve.at(l, 0))
                dve.wait_ge(proj_act.sem, proj_act.at(l, 1))
                c_all = proj[:, :, CQ0:CQ0 + QRANK + KVRANK]
                sqC = sq[:, 0:TT * 384].rearrange("p (t n) -> p t n", t=TT)
                then(dve.tensor_tensor(sqC, c_all, c_all, ALU.mult))
                then(dve.tensor_reduce(ssC, sq[:, 0:TT * 384].rearrange("p (s n) -> p s n", n=P), AX, ALU.add))
                seg = ssC.rearrange("p (t s) -> p t s", t=TT)
                then(dve.tensor_tensor(seg[:, :, 0], seg[:, :, 0], seg[:, :, 1], ALU.add))
                dve.tensor_scalar(varC[:, 0:2], seg[:, :, 0], 1.0 / QRANK, EPS, ALU.mult, ALU.add).then_inc(c_var.sem, 1)
                dve.tensor_scalar(varC[:, 2:4], seg[:, :, 2], 1.0 / KVRANK, EPS, ALU.mult, ALU.add).then_inc(c_var.sem, 1)
                dve.wait_ge(proj_act.sem, proj_act.at(l, 3))
                qk = proj[:, :, 0:V0].rearrange("p t (h d) -> p t h d", d=DA)
                sqA = sq[:, 0:TT * V0].rearrange("p (t n) -> p t n", t=TT)
                then(dve.tensor_tensor(sqA, proj[:, :, 0:V0], proj[:, :, 0:V0], ALU.mult))
                then(dve.tensor_reduce(ssA, sq[:, 0:TT * V0].rearrange("p (h d) -> p h d", d=DA), AX, ALU.add))
                dve.tensor_scalar(varA, ssA, 1.0 / DA, EPS, ALU.mult, ALU.add).then_inc(a_var.sem, 1)
                dve.wait_ge(c_rs.sem, c_rs.at(l, 0))
                for a, b, r in ((CQ0, CKV0, 0), (CKV0, KR0, 2)):
                    part = proj[:, :, a:b]
                    ins = dve.tensor_tensor(part, part, rsC[:, r:r + 2].unsqueeze(2).to_broadcast([P, TT, b - a]), ALU.mult)
                ins.then_inc(c_norm.sem, 1)
                split_mix(KC + 2)
                dve.wait_ge(a_rs.sem, a_rs.at(l, 0))
                dve.tensor_tensor(qk, qk, rsA.rearrange("p (t h) -> p t h", t=TT).unsqueeze(3)
                                  .to_broadcast([P, TT, 10, DA]), ALU.mult).then_inc(a_norm.sem, 1)
                split_mix(KC + 3)
                for c in range(3):
                    if c != 1:
                        dve.wait_ge(c_hi.sem, c_hi.at(l, c // 2))
                    src = ps[:, 3, c * SEQ:(c + 1) * SEQ] if c < 2 else ps[:, 0, 0:SEQ]
                    ins = dve.scalar_tensor_tensor(out=oTl[:, c, :], in0=src, scalar=cols[:, c:c + 1],
                                                   in1=oTh[:, c, :].bitcast(F32), op0=ALU.mult, op1=ALU.subtract)
                    if c != 0:
                        ins.then_inc(c_lo.sem, 1)
                split_mix(UKV)

                dve.wait_ge(trig_done.sem, trig_done.at(l, 0))
                for q in range(2):
                    low, high = (rows[:, q * ROPE + i:q * ROPE + i + 16].unsqueeze(1).to_broadcast([P, TT, 16])
                                 for i in (0, 16))
                    dve.tensor_tensor(cg[:, q, :, 0:16], trig[:, 0, :, :], low, ALU.mult)
                    dve.tensor_tensor(cg[:, q, :, 16:32], trig[:, 0, :, :], high, ALU.mult)
                    dve.scalar_tensor_tensor(out=sg[:, q, :, 0:16], in0=trig[:, 1, :, :], scalar=-1.0, in1=high,
                                             op0=ALU.mult, op1=ALU.mult)
                    dve.tensor_tensor(sg[:, q, :, 16:32], trig[:, 1, :, :], low, ALU.mult)
                then(dve.tensor_scalar(sink8[:, :], rows[:, 2 * ROPE:], 1.0 / SCALE_A, None, ALU.mult))
                kr = proj[:, :, KR0:PROJ_COLS]
                dve.tensor_tensor(krt[:, 0, :, :], kr, cg[:, 1, :, :], ALU.mult)
                dve.tensor_tensor(krt[:, 1, :, 0:16], kr[:, :, 16:32], sg[:, 1, :, 0:16], ALU.mult)
                then(dve.tensor_tensor(krt[:, 1, :, 16:32], kr[:, :, 0:16], sg[:, 1, :, 16:32], ALU.mult))
                then(dve.tensor_tensor(krr[:, :, :], krt[:, 0, :, :], krt[:, 1, :, :], ALU.add))
                then(dve.tensor_tensor(krt[:, 0, :, :], kr, kr, ALU.mult))
                then(dve.tensor_reduce(ssR, krt[:, 0, :, :], AX, ALU.add))
                split_mix(UQ)

                def scores(br, heads):
                    for h in heads:
                        dve.wait_ge(s_ps.sem, s_ps.at(l, br * HB + h))
                        src = ps[:, 4 + h % 4, 0:SEGS * P]
                        if br == 0:
                            slope = 2.0 ** (-8.0 * (h + 1) / HA) / SCALE_A
                            ins = dve.scalar_tensor_tensor(out=S[:, h, :], in0=negdist[:, :], scalar=slope, in1=src,
                                                           op0=ALU.mult, op1=ALU.add)
                        else:
                            ins = dve.tensor_tensor(S[:, h, :], src, maskB[:, :], ALU.add)
                        ins.then_inc(s_sb.sem, 1)

                def tops(br, half):
                    g = HB // 2
                    heads, cells = slice(half * g, (half + 1) * g), slice(half * g * TT, (half + 1) * g * TT)
                    dve.wait_ge(s_sb.sem, s_sb.at(l, br * HB + heads.stop - 1))
                    m = mx[:, heads.start * SEGS:heads.stop * SEGS]
                    then(dve.tensor_reduce(m, S[:, heads, :].rearrange("p h (s k) -> p (h s) k", k=P), AX, ALU.max))
                    m3 = m.rearrange("p (h s) -> p h s", s=SEGS)
                    t2 = top[:, cells].rearrange("p (h t) -> p h t", t=TT)
                    if br == 0:
                        dve.tensor_tensor(t2[:, :, 0], m3[:, :, 0], sink8[:, heads], ALU.max)
                        then(dve.tensor_tensor(m3[:, :, 1], m3[:, :, 1], sink8[:, heads], ALU.max))
                    else:
                        then(dve.tensor_copy(t2[:, :, 0], m3[:, :, 0]))
                    then(dve.tensor_tensor(t2[:, :, 1], m3[:, :, 1], m3[:, :, 2], ALU.max))
                    ins = dve.tensor_scalar(ntop[:, cells], top[:, cells], -(SCALE_A, SCALE_B)[br], None, ALU.mult)
                    if br == 0:
                        then(ins)
                        ins = dve.tensor_tensor(sinkx[:, cells].rearrange("p (h t) -> p h t", t=TT),
                                                ntop[:, cells].rearrange("p (h t) -> p h t", t=TT),
                                                rows[:, 2 * ROPE + heads.start:2 * ROPE + heads.stop].unsqueeze(2)
                                                .to_broadcast([P, g, TT]), ALU.add)
                    ins.then_inc(top_done.sem, 1)

                dve.wait_ge(tab.sem, TAB_STEPS)
                scores(0, range(HB))
                split_mix(GATE4)
                tops(0, 0)
                split_mix(GATE4 + 1)
                dve.wait_ge(q_sq.sem, q_sq.at(l, 0))
                dve.tensor_reduce(ssQ, sq[:, :].rearrange("p (h d) -> p h d", d=QKB), AX, ALU.add).then_inc(q_ss.sem, 1)
                dve.wait_ge(q_ss.sem, q_ss.at(l, 0))
                dve.tensor_scalar(varQ, ssQ, 1.0 / QKB, EPS, ALU.mult, ALU.add).then_inc(q_var.sem, 1)
                tops(0, 1)
                dve.wait_ge(k_sq.sem, k_sq.at(l, 0))
                then(dve.tensor_reduce(ssK, sq[:, 0:2 * HALF].rearrange("p (h d) -> p h d", d=NOPE), AX, ALU.add))
                ssK2 = ssK.rearrange("p (t h) -> p t h", t=TT)
                then(dve.tensor_tensor(ssK2, ssK2, ssR.unsqueeze(2).to_broadcast([P, TT, HB]), ALU.add))
                dve.tensor_scalar(varK, ssK, 1.0 / QKB, EPS, ALU.mult, ALU.add).then_inc(k_var.sem, 1)
                split_mix(GATE4 + 2)
                dve.wait_ge(q_rs.sem, q_rs.at(l, 0))
                then(dve.tensor_tensor(qB.rearrange("p t (b h d) -> p (t b) h d", b=2, d=QKB),
                                       ps[:, 4:8, 0:HB * QKB // 2].rearrange("p b (h d) -> p b h d", d=QKB),
                                       rsQ.rearrange("p (b h) -> p b h", b=4).unsqueeze(3).to_broadcast([P, 4, 4, QKB]),
                                       ALU.mult))
                qh = qB.rearrange("p t (h d) -> p t h d", d=QKB)
                rot = [sq[:, i * 512:(i + 1) * 512].rearrange("p (t h d) -> p t h d", t=TT, h=HB) for i in range(2)]
                for t in range(TT):
                    dve.tensor_tensor(rot[0][:, t], qh[:, t, :, NOPE:], cg[:, 0, t, :].unsqueeze(1).to_broadcast([P, HB, ROPE]),
                                      ALU.mult)
                    dve.tensor_tensor(rot[1][:, t, :, 0:16], qh[:, t, :, NOPE + 16:],
                                      sg[:, 0, t, 0:16].unsqueeze(1).to_broadcast([P, HB, 16]), ALU.mult)
                    ins = dve.tensor_tensor(rot[1][:, t, :, 16:32], qh[:, t, :, NOPE:NOPE + 16],
                                            sg[:, 0, t, 16:32].unsqueeze(1).to_broadcast([P, HB, 16]), ALU.mult)
                then(ins)
                dve.tensor_tensor(qh[:, :, :, NOPE:], rot[0], rot[1], ALU.add).then_inc(q_rot.sem, 1)
                dve.wait_ge(k_rs.sem, k_rs.at(l, 0))
                kh = kB.rearrange("p t (h d) -> p t h d", d=QKB)
                rk = rsK.rearrange("p (t h) -> p t h", t=TT).unsqueeze(3)
                dve.tensor_tensor(kh[:, :, :, 0:NOPE], ps[:, 0:2, :].rearrange("p t (h d) -> p t h d", d=NOPE),
                                  rk.to_broadcast([P, TT, HB, NOPE]), ALU.mult)
                dve.tensor_tensor(kh[:, :, :, NOPE:], krr[:, :, :].unsqueeze(2).to_broadcast([P, TT, HB, ROPE]),
                                  rk.to_broadcast([P, TT, HB, ROPE]), ALU.mult).then_inc(k_norm.sem, 1)
                split_mix(GATE4 + 3)

                def row_sums(br):
                    dve.wait_ge(p_done.sem, p_done.at(l, br * HB + HB - 1))
                    if br == 0:
                        dve.wait_ge(sink_out.sem, sink_out.at(l, 0))
                        then(dve.tensor_tensor(den, den, esink[:, :], ALU.add))
                    dve.reciprocal(rden2[:, br, :], den).then_inc(rden_done.sem, 1)

                def copy_pt(br):
                    for h in range(4 - 4 * br, HB - 4 * br):
                        dve.wait_ge(pt_ps.sem, pt_ps.at(l, br * HB + h))
                        dve.tensor_copy(PT[:, h, :], ps[:, 4 + h % 4, 0:SEGS * P]).then_inc(pt_dve.sem, 1)

                def o_scale(br):
                    dve.wait_ge(rden_done.sem, rden_done.at(l, br))
                    r2 = rden2[:, br, :].rearrange("p (h t) -> p h t", t=TT)
                    for t in range(TT):
                        dve.wait_ge(o_ps.sem, o_ps.at(l, 2 * br + t))
                        dve.tensor_tensor(O[:, t, :].rearrange("p (h d) -> p h d", d=VB),
                                          ps[:, t, :].rearrange("p (h d) -> p h d", d=VB),
                                          r2[:, :, t].unsqueeze(2).to_broadcast([P, HB, VB]), ALU.mult)\
                           .then_inc(o_done.sem, 1)

                def o_low(br):
                    for c in range(2):
                        dve.wait_ge(ot_hi.sem, ot_hi.at(l, 2 * br + c))
                        part = slice(4 * br + 2 * c, 4 * br + 2 * c + 2)
                        dve.tensor_tensor(oTl[:, part, :].rearrange("p c n -> p (c n)"), ps[:, 4 * br + c, :],
                                          oTh[:, part, :].rearrange("p c n -> p (c n)").bitcast(F32),
                                          ALU.subtract).then_inc(ot_lo.sem, 1)

                def branch_ready(br, p):
                    if p % 2 == 0:
                        dve.wait_ge(br_ps.sem, br_ps.at(l, br * 2 + p // 2))
                    else:
                        dve.wait_ge(gu_used.sem, gu_used.at(l, MIX0 + BRANCH + br * 2 + p // 2))

                def gate_a(p):
                    branch_ready(0, p)
                    dve.wait_ge(tanh_done.sem, tanh_done.at(l, 2 * p + 1))
                    part = SG[:, 2 * p:2 * p + 2, 0:SEQ]
                    dve.scalar_tensor_tensor(out=part, in0=part, scalar=1.0, in1=ps[:, p, :].rearrange("p (c n) -> p c n", c=2),
                                             op0=ALU.add, op1=ALU.mult).then_inc(gated_a.sem, 1)

                def merge_b(p):
                    branch_ready(1, p)
                    m = merge[:, p % 2, :]
                    m2 = m.rearrange("p (c n) -> p c n", c=2)
                    dve.scalar_tensor_tensor(out=m2, in0=SG[:, 2 * p:2 * p + 2, SEQ:], scalar=1.0,
                                             in1=ps[:, p, :].rearrange("p (c n) -> p c n", c=2),
                                             op0=ALU.add, op1=ALU.mult).then_inc(gated_b.sem, 1)
                    dve.wait_ge(gated_b.sem, gated_b.at(l, p))
                    dve.tensor_tensor(m2, m2, SG[:, 2 * p:2 * p + 2, 0:SEQ], ALU.add).then_inc(merged.sem, 1)
                    dve.wait_ge(m_hi.sem, m_hi.at(l, p))
                    dve.tensor_tensor(hTl[:, 2 * p:2 * p + 2, :].rearrange("p c n -> p (c n)"), m,
                                      hTh[:, 2 * p:2 * p + 2, :].rearrange("p c n -> p (c n)").bitcast(F32), ALU.subtract)\
                       .then_inc(m_lo.sem, 1)

                for f in range(4):
                    dve.wait_ge(b_ps.sem, b_ps.at(l, 4 + f))
                    dve.tensor_scalar(kTB[:, 2 * f:2 * f + 2, :].rearrange("p h n -> p (h n)"),
                                      ps[0:QKB, LATENT_BANK[4 + f], :], cols[0:QKB, 6:7], None, ALU.mult)\
                       .then_inc(bk_T.sem, 1)
                row_sums(0)
                split_mix(BRANCH)
                copy_pt(0)
                o_scale(0)
                scores(1, range(4))
                o_low(0)
                tops(1, 0)
                scores(1, range(4, HB))
                tops(1, 1)
                gate_a(0)
                gate_a(1)
                copy_pt(1)
                split_mix(BRANCH + 1)
                split_mix(BRANCH + 2)
                row_sums(1)
                o_scale(1)
                split_mix(BRANCH + 3)
                gate_a(2)
                o_low(1)
                gate_a(3)
                split_mix(OUT)
                merge_b(0)
                merge_b(1)
                split_mix(OUT + 1)
                merge_b(2)
                merge_b(3)
                split_mix(OUT + 2)
                split_mix(OUT + 3)
                assert chain[0] == v.per_layer, chain[0]
                ffn(1, FFN2_0)
                residual(2, 0.5)

        @block.tensor
        def _(pe):
            def mm(dst, w, m, start, stop):
                return pe.matmul(dst, w, m, start=start, stop=stop, skip_group_check=True)

            def weight_by_act(dst, wh, wl, mh, ml, start, stop):
                mm(dst, wh, mh, start, False)
                mm(dst, wh, ml, False, False)
                return mm(dst, wl, mh, False, stop)

            def act_by_weight(dst, ah, al, wh, wl, start, stop):
                mm(dst, ah, wh, start, False)
                mm(dst, ah, wl, False, False)
                return mm(dst, al, wh, False, stop)

            def keep_warm(n):
                for _ in range(n):
                    pe.matmul(ps[:, 2, 0:P], ident[:, :], ident[:, :], start=True, stop=True, skip_group_check=True)

            pe.wait_ge(ident_in.sem, 16)
            keep_warm(18)
            with pe.Fori(0, DEPTH) as l:
                def norm_transpose(n):
                    keep_warm(11)
                    pe.wait_ge(diag_done.sem, diag_done.at(l, TT * n + TT - 1))
                    for c in range(KC):
                        for t in range(TT):
                            ins = mm(ps[:, c // 2, (c % 2) * SEQ + t * P:(c % 2) * SEQ + (t + 1) * P],
                                     x[:, t, c * P:(c + 1) * P], diag[:, t, :], True, True)
                        if c % 2:
                            ins.then_inc(ht_ps.sem, 1)

                def block_ready(o):
                    pe.wait_ge(lo_gu.sem, lo_gu.at(l, o))
                    return mix_hi[(o - MIX0) % MIX_SLOTS], mix_lo[(o - MIX0) % MIX_SLOTS]

                def gate_up(i2, o, e, b, first=False):
                    pe.wait_ge(lo_gu.sem, l * BLOCKS + i2 + (o + 3))
                    pe.wait_ge(prod_done.sem, l * (2 * FB) + i2 + (e + 1))
                    for s in range(2):
                        for k in range(KC):
                            if first and s == 0 and k % 2 == 0:
                                pe.wait_ge(ht_lo.sem, ht_lo.at(l, first - 1 + k // 2))
                            c = (s * KC + k) * P
                            ins = weight_by_act(ps[:, b, s * SEQ:(s + 1) * SEQ], wh_gu[b][:, c:c + P], wl_gu[b][:, c:c + P],
                                                hTh[:, k, :], hTl[:, k, :], k == 0, k == KC - 1)
                    ins.then_inc(gu_used.sem, 1)

                def down(i2, e, b, start=False, stop=False):
                    pe.wait_ge(lo_d.sem, l * (2 * FB) + i2 + (e + 3))
                    pe.wait_ge(a_lo.sem, l * (2 * FB) + i2 + (e + 1))
                    for t in range(TT):
                        for h in range(2):
                            ins = act_by_weight(ps[:, 4 + 2 * t + h, :], aTh[:, b, t * P:(t + 1) * P],
                                                aTl[:, b, t * P:(t + 1) * P], wh_d[b][:, h * HALF:(h + 1) * HALF],
                                                wl_d[b][:, h * HALF:(h + 1) * HALF], start, stop)
                            if stop and 2 * t + h < 3:
                                ins.then_inc(acc_done.sem, 1)
                    ins.then_inc(d_used.sem, 1)

                def ffn(w, o0):
                    e0 = w * FB
                    norm_transpose(2 * w)
                    gate_up(0, o0, e0, 0, first=8 * w + 1)
                    gate_up(0, o0 + 1, e0 + 1, 1)
                    down(0, e0, 0, start=True)
                    with pe.Fori(0, FB // 2 - 1) as i:
                        for b in range(2):
                            gate_up(i * 2, o0 + 2 + b, e0 + 2 + b, b)
                            down(i * 2, e0 + 1 + b, 1 - b)
                    down(0, e0 + FB - 1, 1, stop=True)

                ffn(0, 0)
                norm_transpose(1)
                for k in range(KC):
                    o = MIX0 + k
                    hi, lo = block_ready(o)
                    if k % 2 == 0:
                        pe.wait_ge(ht_lo.sem, ht_lo.at(l, 4 + k // 2))
                    for t in range(TT):
                        for g, (a, b) in enumerate(((0, 512), (512, 1024), (1024, PROJ_COLS))):
                            dst = ps[:, 4 + 2 * t + g, :] if g < 2 else ps[:, 0, t * (b - a):(t + 1) * (b - a)]
                            ins = act_by_weight(dst, hTh[:, k, t * P:(t + 1) * P], hTl[:, k, t * P:(t + 1) * P],
                                                hi[:, a:b], lo[:, a:b],
                                                k == 0 and not (g == 2 and t == 1), k == KC - 1)
                    ins.then_inc(gu_used.sem, 1)

                def gates(j):
                    hi, lo = block_ready(at_block("gate", j))
                    if j in (2, 3, 6, 7):
                        pe.wait_ge(tanh_done.sem, tanh_done.at(l, j - 2))
                    elif j in (4, 5):
                        pe.wait_ge(v_copied.sem, v_copied.at(l, j - 4))
                    for s in range(2):
                        for c in range(KC):
                            a = (s * KC + c) * P
                            ins = weight_by_act(ps[:, GATE_BANK[j], s * SEQ:(s + 1) * SEQ], hi[:, a:a + P], lo[:, a:a + P],
                                                hTh[:, c, :], hTl[:, c, :], c == 0, c == KC - 1)
                    ins.then_inc(gu_used.sem, 1)

                gates(0)
                gates(1)
                pe.wait_ge(c_norm.sem, c_norm.at(l, 0))
                for c in range(3):
                    for t in range(TT):
                        dst = ps[:, 3, c * SEQ + t * P:c * SEQ + (t + 1) * P] if c < 2 else ps[:, 0, t * P:(t + 1) * P]
                        ins = pe.transpose(dst, proj[:, t, CQ0 + c * P:CQ0 + (c + 1) * P], ident[:, :])
                    if c > 0:
                        ins.then_inc(c_ps.sem, 1)
                gates(2)
                pe.wait_ge(a_norm.sem, a_norm.at(l, 0))
                for c in range(5):
                    for t in range(TT):
                        ins = pe.transpose(ps[:, 4 + c // 2, (c % 2) * SEQ + t * P:(c % 2) * SEQ + (t + 1) * P],
                                           proj[:, t, c * P:(c + 1) * P], ident[:, :])
                ins.then_inc(a_ps.sem, 1)
                gates(3)

                def scores(br, heads):
                    for h in heads:
                        if h >= 4:
                            pe.wait_ge(s_sb.sem, s_sb.at(l, br * HB + h - 4))
                        elif br == 0:
                            pe.wait_ge(a_T.sem, a_T.at(l, 2))
                        else:
                            pe.wait_ge(*pt_copied(l, 0, h + 4))
                        if br == 0:
                            r = slice(DA * (h // GA), DA * (h // GA + 1))
                            q, k = qTA[r, h % GA, :], kTA[r, :]
                        else:
                            q, k = qTB[:, h, :], kTB[:, h, :]
                        mm(ps[:, 4 + h % 4, 0:P], q[:, 0:P], k[:, 0:P], True, True)
                        mm(ps[:, 4 + h % 4, P:SEGS * P], q[:, P:SEQ], k, True, True).then_inc(s_ps.sem, 1)

                scores(0, range(HB))
                hi, lo = block_ready(at_block("ukv", 0))
                pe.wait_ge(c_lo.sem, c_lo.at(l, 1))
                pe.wait_ge(tanh_done.sem, tanh_done.at(l, 3))
                for t in range(TT):
                    for h, bank in enumerate(((0, 3), (1, 2))[t]):
                        ins = act_by_weight(ps[:, bank, :], oTh[:, 2, t * P:(t + 1) * P], oTl[:, 2, t * P:(t + 1) * P],
                                            hi[:, h * HALF:(h + 1) * HALF], lo[:, h * HALF:(h + 1) * HALF],
                                            True, True)
                ins.then_inc(gu_used.sem, 1)
                hi, lo = block_ready(at_block("uq", 0))
                pe.wait_ge(s_sb.sem, s_sb.at(l, HB - 1))
                half = HB * QKB // 2
                for t in range(TT):
                    for h in range(2):
                        for c in range(2):
                            a = c * HB * QKB + h * half
                            ins = act_by_weight(ps[:, 4 + 2 * t + h, 0:half], oTh[:, c, t * P:(t + 1) * P],
                                                oTl[:, c, t * P:(t + 1) * P], hi[:, a:a + half],
                                                lo[:, a:a + half], c == 0, c == 1)
                ins.then_inc(gu_used.sem, 1)
                gates(4)
                gates(5)

                def transpose_p(br):
                    for h in range(HB):
                        pe.wait_ge(p_done.sem, p_done.at(l, br * HB + h))
                        if h >= 4:
                            pe.wait_ge(*pt_copied(l, br, h - 4))
                        elif br == 0:
                            if h == 0:
                                pe.wait_ge(bk_T.sem, bk_T.at(l, 3))
                            pe.wait_ge(bq_T.sem, bq_T.at(l, h))
                        else:
                            pe.wait_ge(s_sb.sem, s_sb.at(l, HB + h + 4))
                        for s in range(SEGS):
                            ins = pe.transpose(ps[:, 4 + h % 4, s * P:(s + 1) * P], S[:, h, s * P:(s + 1) * P], ident[:, :])
                        ins.then_inc(pt_ps.sem, 1)

                def values(br):
                    for h in range(HB):
                        pe.wait_ge(*pt_copied(l, br, h))
                        for t in range(TT):
                            dst = ps[:, t, h * VB:(h + 1) * VB]
                            for i, seg in enumerate(((0,), (1, 2))[t]):
                                if br == 0:
                                    val = proj[:, i, V0 + DA * (h // GA):V0 + DA * (h // GA + 1)]
                                else:
                                    val = vB[:, i, h * VB:(h + 1) * VB]
                                ins = mm(dst, PT[:, h, seg * P:(seg + 1) * P], val, i == 0, i == t)
                            if h == HB - 1:
                                ins.then_inc(o_ps.sem, 1)

                def transpose_o(br):
                    pe.wait_ge(o_done.sem, o_done.at(l, 2 * br + TT - 1))
                    for t in range(TT):
                        for c in range(4):
                            ins = pe.transpose(ps[:, 4 * br + c // 2, (c % 2) * SEQ + t * P:(c % 2) * SEQ + (t + 1) * P],
                                               O[:, t, c * P:(c + 1) * P], ident[:, :])
                            if t == TT - 1 and c % 2:
                                ins.then_inc(ot_ps.sem, 1)

                gates(6)
                pe.wait_ge(q_rot.sem, q_rot.at(l, 0))
                for f in range(8):
                    if f == 4:
                        pe.wait_ge(k_norm.sem, k_norm.at(l, 0))
                    if f == 6:
                        pe.wait_ge(tanh_done.sem, tanh_done.at(l, 6))
                    if f == 7:
                        pe.wait_ge(bq_T.sem, bq_T.at(l, 0))
                    for h in (2 * (f % 4), 2 * (f % 4) + 1):
                        for t in range(TT):
                            src = (qB if f < 4 else kB)[:, t, h * QKB:(h + 1) * QKB]
                            ins = pe.transpose(ps[0:QKB, LATENT_BANK[f], (h % 2) * SEQ + t * P:(h % 2) * SEQ + (t + 1) * P],
                                               src, ident[:, :])
                    ins.then_inc(b_ps.sem, 1)
                def branches(br, p):
                    hi, lo = block_ready(MIX0 + BRANCH + 2 * br + p // 2)
                    for j in range(2):
                        for c in range(4):
                            a = (((p % 2) * 2 + j) * 4 + c) * P
                            ins = weight_by_act(ps[:, p, j * SEQ:(j + 1) * SEQ], hi[:, a:a + P], lo[:, a:a + P],
                                                oTh[:, 4 * br + c, :], oTl[:, 4 * br + c, :], c == 0, c == 3)
                    ins.then_inc((br_ps, gu_used)[p % 2].sem, 1)

                gates(7)
                transpose_p(0)
                values(0)
                scores(1, range(4))
                transpose_o(0)
                scores(1, range(4, HB))
                pe.wait_ge(ot_lo.sem, ot_lo.at(l, 1))
                branches(0, 0)
                branches(0, 1)
                transpose_p(1)
                pe.wait_ge(gated_a.sem, gated_a.at(l, 1))
                values(1)
                pe.wait_ge(tanh_done.sem, tanh_done.at(l, 7))
                branches(0, 2)
                transpose_o(1)
                branches(0, 3)
                pe.wait_ge(ot_lo.sem, ot_lo.at(l, 3))
                branches(1, 0)
                branches(1, 1)
                pe.wait_ge(gated_a.sem, gated_a.at(l, 3))
                branches(1, 2)
                branches(1, 3)
                for j in range(4):
                    hi, lo = block_ready(MIX0 + OUT + j)
                    pe.wait_ge(m_lo.sem, m_lo.at(l, j))
                    for t in range(TT):
                        for h in range(2):
                            for c in range(2):
                                a = c * D_MODEL + h * HALF
                                ins = act_by_weight(ps[:, 4 + 2 * t + h, :], hTh[:, 2 * j + c, t * P:(t + 1) * P],
                                                    hTl[:, 2 * j + c, t * P:(t + 1) * P], hi[:, a:a + HALF],
                                                    lo[:, a:a + HALF], j == 0 and c == 0, j == 3 and c == 1)
                            if j == 3 and 2 * t + h < 3:
                                ins.then_inc(acc_done.sem, 1)
                    ins.then_inc(gu_used.sem, 1)
                ffn(1, FFN2_0)


def kernel(**inputs):
    import concourse.bacc as bacc
    from concourse.bass_utils import run_bass_kernel_spmd

    a = {k: np.asarray(v) for k, v in inputs.items()}
    L, f32 = DEPTH, np.float32

    def tiles(w, cols):
        n = w.shape[2] // cols
        return w.reshape(L, w.shape[1] // P, P, n, cols).transpose(0, 3, 2, 1, 4)

    def ffn_blocks(name):
        gate, up = (tiles(a[f"{name}_w_{part}"], P).reshape(L, FB, P, KC * P) for part in ("gate", "up"))
        down = a[f"{name}_w_down"].reshape(L, FB, P, D_MODEL)
        return np.concatenate([gate, up, down], axis=3)

    order = np.arange(HA).reshape(2, GA).T.ravel()
    w_in = a["w_in"]
    q_cols = w_in[:, :, :HA * DA].reshape(L, D_MODEL, HA, DA)[:, :, order].reshape(L, D_MODEL, HA * DA)
    gates = w_in[:, :, PROJ_COLS:]
    gate_blocks = np.concatenate([tiles(gates[:, :, :D_MODEL], P).reshape(L, KC, P, KC * P),
                                  tiles(gates[:, :, D_MODEL:], P).reshape(L, KC, P, KC * P)], axis=3)
    ukv = a["mla_w_ukv"].reshape(L, KVRANK, HB, NOPE + VB)
    branch = np.stack([tiles(a["w_branch_a"], P), tiles(a["w_branch_b"], P)], axis=1)
    branch = branch.reshape(L, 2, 2, 4, P, 4 * P).transpose(0, 1, 2, 4, 3, 5)
    idx = np.arange(P)
    causal = np.where(idx[None, :] <= idx[:, None], 0.0, NEG).astype(f32)
    previous = np.where(idx[None, :] > idx[:, None], 0.0, NEG).astype(f32)
    zero = np.zeros((P, P), f32)
    eye = np.concatenate([np.eye(P, dtype=f32), zero, zero], axis=1)
    ones = np.ones((L, ROPE), f32)
    two = lambda g: np.concatenate([g, g], axis=1)
    nope = lambda g: np.concatenate([g[:, :NOPE], ones, np.zeros((L, P - QKB), f32)], axis=1)
    norms = np.stack([a["ffn1_norm"], a["mix_norm"], a["ffn2_norm"]], axis=1)
    spare = lambda rows: np.concatenate([rows, np.zeros_like(rows[:1])])
    arrays = {
        "x": a["x"],
        "positions": a["positions"],
        "gain_cols": spare(np.concatenate([np.stack([
            a["mla_q_lora_norm"][:, :P], a["mla_q_lora_norm"][:, P:], a["mla_kv_lora_norm"], two(a["swa_q_norm"]),
            two(a["swa_k_norm"]), nope(a["mla_q_norm"]), nope(a["mla_k_norm"])], axis=2),
            norms.reshape(L, 3 * KC, P).transpose(0, 2, 1)], axis=2)),
        "gain_rows": spare(np.concatenate([a["mla_q_norm"][:, NOPE:], a["mla_k_norm"][:, NOPE:], a["swa_sinks"]], axis=1)),
        "w_ffn": np.stack([ffn_blocks("ffn1"), ffn_blocks("ffn2")], axis=1).reshape(2 * L * FB, P, GU_COLS + DN_COLS),
        "w_proj": np.concatenate([q_cols, w_in[:, :, HA * DA:PROJ_COLS]], axis=2).reshape(L * KC, P, PROJ_COLS),
        "w_gate": gate_blocks.reshape(L * KC, P, GU_COLS),
        "w_uq": a["mla_w_uq"].reshape(L, 2, P, HB * QKB).transpose(0, 2, 1, 3).reshape(L, P, UQ_COLS),
        "w_ukv": ukv.reshape(L, KVRANK, HB, 2, NOPE).transpose(0, 1, 3, 2, 4).reshape(L, P, UKV_COLS),
        "w_branch": branch.reshape(4 * L, P, GU_COLS),
        "w_out": a["w_out"].reshape(L, 4, 2, P, D_MODEL).transpose(0, 1, 3, 2, 4).reshape(4 * L, P, GU_COLS),
        "masks": np.stack([eye, np.concatenate([causal, previous, causal], axis=1),
                           np.concatenate([causal, zero, causal], axis=1)]),
        "inv_freq": np.tile((10000.0 ** (-np.arange(16, dtype=f32) / f32(16))).astype(f32), (P, 1)),
    }
    nc = bacc.Bacc("TRN2", target_bir_lowering=False, num_devices=1)
    arrays = {k: np.ascontiguousarray(v) for k, v in arrays.items()}
    args = [nc.dram_tensor(f"in_{k}", v.shape, mybir.dt.from_np(v.dtype), kind="ExternalInput").ap() for k, v in arrays.items()]
    args.append(nc.dram_tensor("out", (1, SEQ, D_MODEL), F32, kind="ExternalOutput").ap())
    build(nc, *args)
    return run_bass_kernel_spmd(nc, [{f"in_{k}": v for k, v in arrays.items()}], core_ids=[0]).results[0]["out"]
```
